# Optimizing a Trainium2 kernel written in Bass

```python
import jax, jax.numpy as jnp
from jax import lax
import numpy as np

D_MODEL = 1024
BATCH = 1
SEQ = 512
DEPTH = 2

CHUNK = 64
EPS = 1e-6
NEG = -1e30
A_HEADS = 8
A_KV_HEADS = 2
A_HEAD_DIM = 64
A_WINDOW = 128
A_WIN_CHUNKS = A_WINDOW // CHUNK
A_Q_W = A_HEADS * A_HEAD_DIM
A_KV_W = A_KV_HEADS * A_HEAD_DIM
B_HEADS = 8
B_Q_RANK = 384
B_KV_RANK = 256
B_NOPE_DIM = 64
B_ROPE_DIM = 32
B_V_DIM = 64
B_OUT_W = B_HEADS * B_V_DIM
ROPE_THETA = 10000.0
Q_BLOCK = 128
IN_W = A_Q_W + 2 * A_KV_W + B_Q_RANK + B_KV_RANK + B_ROPE_DIM
N_GROUPS = 8
EXPERTS_PER_GROUP = 8
N_EXPERTS = N_GROUPS * EXPERTS_PER_GROUP
TOP_K = 2
D_EXPERT = 256
MOE_BLOCK = 128

kernel_name = "hybrid_swa_mla_hmoe_trunk"

def rmsnorm(x, g):
    xf = x.astype(jnp.float32)
    y = xf * lax.rsqrt(jnp.mean(xf * xf, axis=-1, keepdims=True) + EPS)
    return (y * g.astype(jnp.float32)).astype(x.dtype)

def alibi_slopes(n_heads):
    return jnp.exp2(-8.0 * jnp.arange(1, n_heads + 1, dtype=jnp.float32) / n_heads)

def apply_rope(x, cos, sin):
    x1, x2 = jnp.split(x.astype(jnp.float32), 2, axis=-1)
    return jnp.concatenate([x1 * cos - x2 * sin, x1 * sin + x2 * cos], axis=-1).astype(x.dtype)

def swa_sink_attention(q, k, v, pos, sinks):
    B, S, H, hd = q.shape
    NC = S // CHUNK
    R = H // A_KV_HEADS
    KW = A_WIN_CHUNKS * CHUNK
    qc = q.reshape(B, NC, CHUNK, A_KV_HEADS, R, hd)

    def band(t):
        tc = t.reshape((B, NC, CHUNK) + t.shape[2:])
        parts = []
        for w in range(A_WIN_CHUNKS - 1, 0, -1):
            pad = [(0, 0), (w, 0)] + [(0, 0)] * (tc.ndim - 2)
            parts.append(jnp.pad(tc, pad)[:, :NC])
        parts.append(tc)
        return jnp.concatenate(parts, axis=2)

    kb, vb, pk = band(k), band(v), band(pos)
    s = jnp.einsum('bcqgrd,bckgd->bcgrqk', qc, kb).astype(jnp.float32) * (hd ** -0.5)
    src_chunk = jnp.arange(NC)[:, None] - (A_WIN_CHUNKS - 1) + jnp.arange(KW)[None, :] // CHUNK
    valid = src_chunk >= 0
    pq = pos.reshape(B, NC, CHUNK)
    dist = jnp.abs(pq[:, :, :, None] - pk[:, :, None, :]).astype(jnp.float32)
    slopes = alibi_slopes(H).reshape(A_KV_HEADS, R)
    s = s - slopes[None, None, :, :, None, None] * dist[:, :, None, None, :, :]
    s = jnp.where(valid[None, :, None, None, None, :], s, NEG)
    sink = sinks.astype(jnp.float32).reshape(A_KV_HEADS, R)[None, None, :, :, None, None]
    m = jnp.maximum(jnp.max(s, axis=-1, keepdims=True), sink)
    p = jnp.exp(s - m)
    p = p / (jnp.sum(p, axis=-1, keepdims=True) + jnp.exp(sink - m))
    o = jnp.einsum('bcgrqk,bckgd->bcqgrd', p.astype(v.dtype), vb)
    return o.reshape(B, S, H * hd)

def mla_attention(qn, qr, kn, kr, v):
    B, S, H, _ = qn.shape
    NB = S // Q_BLOCK
    scale = (B_NOPE_DIM + B_ROPE_DIM) ** -0.5
    key_chunk = jnp.arange(S) // CHUNK

    def block(args):
        i, qn_b, qr_b = args
        s = jnp.einsum('bqhd,bkhd->bhqk', qn_b, kn) + jnp.einsum('bqhd,bkd->bhqk', qr_b, kr)
        s = s.astype(jnp.float32) * scale
        q_chunk = (i * Q_BLOCK + jnp.arange(Q_BLOCK)) // CHUNK
        s = jnp.where(key_chunk[None, :] <= q_chunk[:, None], s, NEG)
        p = jax.nn.softmax(s, axis=-1)
        return jnp.einsum('bhqk,bkhd->bqhd', p.astype(v.dtype), v)

    qn_blocks = jnp.moveaxis(qn.reshape(B, NB, Q_BLOCK, H, B_NOPE_DIM), 1, 0)
    qr_blocks = jnp.moveaxis(qr.reshape(B, NB, Q_BLOCK, H, B_ROPE_DIM), 1, 0)
    o = lax.map(block, (jnp.arange(NB), qn_blocks, qr_blocks))
    return jnp.moveaxis(o, 0, 1).reshape(B, S, H * B_V_DIM)

def hierarchical_moe(x, w_group, b_group, w_er, b_er, w1, w3, w2):
    B, S, D = x.shape
    xt = x.reshape(-1, D)
    N = xt.shape[0]
    g_logits = (xt @ w_group + b_group).astype(jnp.float32)
    g_prob = jax.nn.softmax(g_logits, axis=-1)
    grp = jnp.argmax(g_logits, axis=-1)
    p_grp = jnp.take_along_axis(g_prob, grp[:, None], axis=-1)
    e_logits = (xt @ w_er + b_er).astype(jnp.float32).reshape(N, N_GROUPS, EXPERTS_PER_GROUP)
    e_logits = jnp.take_along_axis(e_logits, grp[:, None, None], axis=1)[:, 0]
    top_val, top_idx = lax.top_k(e_logits, TOP_K)
    comb = jax.nn.softmax(top_val, axis=-1) * p_grp
    expert_id = grp[:, None] * EXPERTS_PER_GROUP + top_idx

    A = N * TOP_K
    e_flat = expert_id.reshape(-1)
    tok = jnp.repeat(jnp.arange(N), TOP_K)
    wt = comb.reshape(-1)
    order = jnp.argsort(e_flat)
    e_s, tok_s, wt_s = e_flat[order], tok[order], wt[order]
    counts = jnp.zeros((N_EXPERTS,), jnp.int32).at[e_flat].add(1)
    start = jnp.cumsum(counts) - counts
    padded = (counts + MOE_BLOCK - 1) // MOE_BLOCK * MOE_BLOCK
    pend = jnp.cumsum(padded)
    pstart = pend - padded
    dest = pstart[e_s] + (jnp.arange(A) - start[e_s])
    n_blocks = -(-A // MOE_BLOCK) + N_EXPERTS
    cap = n_blocks * MOE_BLOCK
    xbuf = jnp.zeros((cap, D), x.dtype).at[dest].set(xt[tok_s])
    blk_expert = jnp.minimum(jnp.searchsorted(pend, jnp.arange(n_blocks) * MOE_BLOCK, side='right'), N_EXPERTS - 1)

    def run(args):
        e, xb = args
        h = jax.nn.silu(xb @ w1[e]) * (xb @ w3[e])
        return h @ w2[e]

    ybuf = lax.map(run, (blk_expert, xbuf.reshape(n_blocks, MOE_BLOCK, D))).reshape(cap, D)
    y = jax.ops.segment_sum(ybuf[dest] * wt_s[:, None].astype(x.dtype), tok_s, num_segments=N)
    return y.reshape(B, S, D)

def setup_inputs(seed: int = 0) -> dict:
    key = jax.random.key(seed)
    ks = jax.random.split(key, 32)
    f32 = jnp.float32

    def nrm(k, shape, fan_in):
        return jax.random.normal(k, shape, f32) * (fan_in ** -0.5)

    def gain(k, shape):
        return 1.0 + 0.01 * jax.random.normal(k, shape, f32)

    L, D = DEPTH, D_MODEL
    offset = jax.random.randint(ks[1], (BATCH, 1), 0, 4096, dtype=jnp.int32)
    positions = offset + jnp.arange(SEQ, dtype=jnp.int32)[None, :]
    return {
        "x": jax.random.normal(ks[0], (BATCH, SEQ, D), f32),
        "positions": positions,
        "norm_mix": gain(ks[2], (L, D)),
        "w_in": nrm(ks[3], (L, D, IN_W), D),
        "sinks": 0.5 * jax.random.normal(ks[4], (L, A_HEADS), f32),
        "q_norm": gain(ks[5], (L, B_Q_RANK)),
        "w_qb": nrm(ks[6], (L, B_Q_RANK, B_HEADS * (B_NOPE_DIM + B_ROPE_DIM)), B_Q_RANK),
        "kv_norm": gain(ks[7], (L, B_KV_RANK)),
        "w_kvb": nrm(ks[8], (L, B_KV_RANK, B_HEADS * (B_NOPE_DIM + B_V_DIM)), B_KV_RANK),
        "w_gate": nrm(ks[9], (L, D, 2 * D), D),
        "b_gate": 0.01 * jax.random.normal(ks[10], (L, 2 * D), f32),
        "w_oa": nrm(ks[11], (L, A_Q_W, D), A_Q_W),
        "w_ob": nrm(ks[12], (L, B_OUT_W, D), B_OUT_W),
        "w_out": nrm(ks[13], (L, D, D), D),
        "norm_ffn": gain(ks[14], (L, D)),
        "w_group": nrm(ks[15], (L, D, N_GROUPS), D),
        "b_group": 0.01 * jax.random.normal(ks[16], (L, N_GROUPS), f32),
        "w_er": nrm(ks[17], (L, D, N_EXPERTS), D),
        "b_er": 0.01 * jax.random.normal(ks[18], (L, N_EXPERTS), f32),
        "w1": nrm(ks[19], (L, N_EXPERTS, D, D_EXPERT), D),
        "w3": nrm(ks[20], (L, N_EXPERTS, D, D_EXPERT), D),
        "w2": nrm(ks[21], (L, N_EXPERTS, D_EXPERT, D), D_EXPERT),
        "norm_final": gain(ks[22], (D,)),
    }

def reference(x, positions, norm_mix, w_in, sinks, q_norm, w_qb, kv_norm, w_kvb, w_gate, b_gate,
              w_oa, w_ob, w_out, norm_ffn, w_group, b_group, w_er, b_er, w1, w3, w2, norm_final):
    B, S, D = x.shape
    splits = [int(v) for v in np.cumsum([A_Q_W, A_KV_W, A_KV_W, B_Q_RANK, B_KV_RANK])]
    half = B_ROPE_DIM // 2
    inv_freq = ROPE_THETA ** (-jnp.arange(half, dtype=jnp.float32) / half)
    ang = positions.astype(jnp.float32)[..., None] * inv_freq
    cos, sin = jnp.cos(ang), jnp.sin(ang)

    for l in range(DEPTH):
        h = rmsnorm(x, norm_mix[l])
        z = h @ w_in[l]
        aq, ak, av, bq, bkv, bkr = jnp.split(z, splits, axis=-1)

        oa = swa_sink_attention(aq.reshape(B, S, A_HEADS, A_HEAD_DIM),
                                ak.reshape(B, S, A_KV_HEADS, A_HEAD_DIM),
                                av.reshape(B, S, A_KV_HEADS, A_HEAD_DIM),
                                positions, sinks[l])

        qb = (rmsnorm(bq, q_norm[l]) @ w_qb[l]).reshape(B, S, B_HEADS, B_NOPE_DIM + B_ROPE_DIM)
        qn, qr = qb[..., :B_NOPE_DIM], qb[..., B_NOPE_DIM:]
        qr = apply_rope(qr, cos[:, :, None, :], sin[:, :, None, :])
        kvb = (rmsnorm(bkv, kv_norm[l]) @ w_kvb[l]).reshape(B, S, B_HEADS, B_NOPE_DIM + B_V_DIM)
        kn, vb = kvb[..., :B_NOPE_DIM], kvb[..., B_NOPE_DIM:]
        kr = apply_rope(bkr, cos, sin)
        ob = mla_attention(qn, qr, kn, kr, vb)

        gates = jax.nn.sigmoid(h @ w_gate[l] + b_gate[l])
        ga, gb = gates[..., :D], gates[..., D:]
        mix = ga * (oa @ w_oa[l]) + gb * (ob @ w_ob[l])
        x = x + mix @ w_out[l]

        h = rmsnorm(x, norm_ffn[l])
        x = x + hierarchical_moe(h, w_group[l], b_group[l], w_er[l], b_er[l], w1[l], w3[l], w2[l])

    return rmsnorm(x, norm_final)


_drawn_inputs = setup_inputs


def setup_inputs(seed=0):
    import zlib

    import numpy as np

    out = dict(_drawn_inputs(seed))
    spreads = {}
    factors = {'norm_mix': 3.96,
     'sinks': 25.92,
     'q_norm': 8.0,
     'kv_norm': 5.06,
     'b_gate': 8.0,
     'norm_final': 31.902,
     'b_group': 2.719,
     'b_er': 3.174}
    for name, (base, spread) in spreads.items():
        noise = np.random.default_rng([zlib.crc32(name.encode()), seed]).standard_normal(out[name].shape)
        drawn = base * np.exp(spread * noise) if base else spread * noise
        out[name] = __import__('jax').numpy.asarray(drawn.astype(out[name].dtype))
    for name, factor in factors.items():
        out[name] = (out[name] * factor).astype(out[name].dtype)
    return out
```

```python
from contextlib import ExitStack

import numpy as np
import concourse.bass as bass
from concourse import mybir

F32 = mybir.dt.float32
F32R = mybir.dt.float32r
BF16 = mybir.dt.bfloat16
I32 = mybir.dt.int32
ALU = mybir.AluOpType
ACT = mybir.ActivationFunctionType
AX = mybir.AxisListType.X

P = 128
CHUNK = 64
A_KV, A_DIM = 2, 64
ROPE_THETA = 10000.0
EPS = 1e-6
BIG = 1e33
NEG = -1e30
UNIT = 2048
NRAW = 6
NSPL, NSPM = 3, 6
AHEAD = 3
KB = 1024


def hybrid_trunk(nc, x, positions, norm_mix, w_in, sinks, q_norm, w_qb, kv_norm, w_kvb, w_gate, b_gate,
                 w_oa, w_ob, w_out, norm_ffn, w_group, b_group, w_er, b_er, w1, w3, w2, norm_final, out):
    L, D, IN_W = w_in.shape
    T = x.shape[1]
    NT, KD = T // P, D // P
    AH = sinks.shape[1]
    AQ = AH * A_DIM
    QR, KVR = w_qb.shape[1], w_kvb.shape[1]
    HEADS = AH
    ROPE = IN_W - AQ - 2 * A_KV * A_DIM - QR - KVR
    HALF = ROPE // 2
    QD = w_qb.shape[2] // HEADS
    NOPE = QD - ROPE
    VD = w_kvb.shape[2] // HEADS - NOPE
    NG = w_group.shape[2]
    NE = w_er.shape[2] // NG
    FE = w1.shape[3]
    KQ, KKV = QR // P, KVR // P
    KC = KQ + KKV
    ZC = IN_W - AQ - A_KV * A_DIM
    ZQ, ZKV, ZKR = A_KV * A_DIM, A_KV * A_DIM + QR, A_KV * A_DIM + QR + KVR
    KO = AQ // P
    B_SCALE = float(QD) ** -0.5
    A_SCALE = float(A_DIM) ** -0.5
    slopes = [float(np.float32(2.0) ** np.float32(-8.0 * (h + 1) / AH)) for h in range(AH)]
    NOVF = T // P - 1
    NB = NG + NOVF
    NR = NG + NG * NE
    SC = 2 + NE

    xres = nc.dram_tensor("xres", (T, D), F32, kind="Internal").ap()
    hrows = nc.dram_tensor("hrows", (T, D), F32, kind="Internal").ap()
    yrows = nc.dram_tensor("yrows", (T, D), F32, kind="Internal").ap()

    def tiles(ap):
        return ap.rearrange("(t p) d -> p t d", p=P)

    NCOL_T = IN_W - ZC
    plan = [(w_in, k, min(3, KD - k), 0, NCOL_T) for k in range(0, KD, 3)]
    U_Z1 = (0, len(plan))
    plan += [(w_in, k, 2, NCOL_T, ZC) for k in range(0, KD, 2)]
    U_Z2 = (U_Z1[1], len(plan))
    plan += [(w_qb, 0, 2, 0, HEADS * QD), (w_qb, 2, KQ - 2, 0, HEADS * QD), (w_kvb, 0, KKV, 0, HEADS * (NOPE + VD))]
    U_QKV = (U_Z2[1], len(plan))
    plan += [(w_oa, k, 2, 0, D) for k in range(0, KO, 2)]
    U_OA = (U_QKV[1], len(plan))
    plan += [(w_ob, k, 2, 0, D) for k in range(0, KO, 2)]
    U_OB = (U_OA[1], len(plan))
    plan += [(w_gate, k, 2, 0, D) for k in range(0, KD, 2)]
    U_GA = (U_OB[1], len(plan))
    plan += [(w_gate, k, 2, D, D) for k in range(0, KD, 2)]
    U_GB = (U_GA[1], len(plan))
    plan += [(w_out, k, 2, 0, D) for k in range(0, KD, 2)]
    U_OUT = (U_GB[1], len(plan))
    ND = len(plan)
    NU = 3 * NE
    assert NU % NRAW == 0 and NU % NSPM == 0 and AHEAD == NSPL

    moe_units = []
    for e in range(NE):
        moe_units.append(("up", e, 0))
        if e >= 2:
            moe_units.append(("down", e - 2, 0))
        moe_units.append(("up", e, 1))
    moe_units += [("down", NE - 2, 0), ("down", NE - 1, 0)]
    unit_at = {u: i for i, u in enumerate(moe_units)}

    ctx = ExitStack()
    with ctx:
        base = [-(-nc.sbuf_base // 64) * 64]

        def sb(name, shape, dt=F32, at=None):
            size = int(np.prod(shape[1:])) * (2 if dt == BF16 else 4)
            off = base[0] if at is None else region + int(at)
            if at is None:
                base[0] += -(-size // 32) * 32
            else:
                assert off + size <= limit, (name, off + size - limit)
            return nc.alloc_sbuf_tensor_at(name, shape, dt, offset=off)

        def sem(name):
            return ctx.enter_context(nc.semaphore(name))

        limit = nc.sbuf_usable_end - 64
        raw = sb("raw", [P, NRAW, UNIT])
        wh = sb("wh", [P, NSPL, UNIT], F32R)
        wl = sb("wl", [P, NSPL, UNIT], F32R)
        ident = sb("ident", [P, P])
        upper_r = sb("upper_r", [P, P], F32R)
        ones_r = sb("ones_r", [P, P], F32R)
        iota_p = sb("iota_p", [P, P])
        lower8 = sb("lower8", [P, NG, NG])
        iota8 = sb("iota8", [P, NG])
        tokid = sb("tokid", [P, NT])
        iota3 = sb("iota3", [P, NOVF])
        rowsel = sb("rowsel", [1, P], BF16)
        negrow = sb("negrow", [1, CHUNK], BF16)
        gain = sb("gain", [P, D])
        gain_at = base[0] - D * 4
        dist = sb("dist", [P, NT, 2 * P])
        cos = sb("cos", [P, NT, HALF])
        sin = sb("sin", [P, NT, HALF])
        wr = sb("wr", [P, KD, NR])
        br = sb("br", [P, NR])
        bg = sb("bg", [P, 2 * KD])
        gc = sb("gc", [P, KC])
        sink = sb("sink", [P, AH])
        ss = sb("ss", [P, NT])
        vs = sb("vs", [P, NT])
        rs = sb("rs", [P, NT])
        rstd = sb("rstd", [P, NT])
        ss2 = sb("ss2", [P, 2, NT])
        vs2 = sb("vs2", [P, 2, NT])
        rs2 = sb("rs2", [P, 2, NT])
        rstd2 = sb("rstd2", [P, 2, NT])
        slot_tab = sb("slot_tab", [P, NB, SC])
        idx = sb("idx", [P, NB + 1], I32)
        ovf_i = sb("ovf_i", [1, NOVF + 1], I32)
        region = base[0]

        posc_i = sb("posc_i", [P, NT], I32, 49 * KB)
        posr_i = sb("posr_i", [P, T], I32, 50 * KB)
        posc = sb("posc", [P, NT], F32, 52 * KB)
        posr = sb("posr", [P, T], F32, 53 * KB)
        invf = sb("invf", [P, HALF], F32, 56 * KB)
        ang = sb("ang", [P, NT, HALF], F32, 57 * KB)
        trig = [sb(f"trig{i}", [P, NT, HALF], F32, (58 + i) * KB) for i in range(6)]
        upper = sb("upper", [P, P], F32, 64 * KB)
        ones = sb("ones", [P, P], F32, 64.5 * KB)
        xl = sb("xl", [P, NT, D], F32, 80 * KB)
        x1 = sb("x1", [P, NT, D], F32, 0)
        sq1 = sb("sq1", [P, NT, D], F32, 32 * KB)
        h1h = sb("h1h", [P, KD, T], F32R, 16 * KB)
        h1l = sb("h1l", [P, KD, T], F32R, 32 * KB)
        aq = sb("aq", [P, AH // 2, T], F32, 48 * KB)
        ak = sb("ak", [P, T], F32, 56 * KB)
        z = sb("z", [P, NT, ZC], F32, 58 * KB)
        sqz = sb("sqz", [P, NT, QR + KVR], F32, 72 * KB)
        ch = sb("ch", [P, KC, T], F32R, 0)
        cl = sb("cl", [P, KC, T], F32R, 10 * KB)
        v = sb("v", [P, NT, HEADS * VD], F32, 20 * KB)
        qt = sb("qt", [P, HEADS, T], F32, 28 * KB)
        kt = sb("kt", [P, HEADS, T], F32, 72 * KB)
        qc = [sb(f"qc{i}", [P, HEADS, QD], F32, (88 + 3 * i) * KB) for i in range(2)]
        kc = [sb("kc0", [P, HEADS, QD], F32, 94 * KB), sb("kc1", [P, HEADS, QD], F32, 44 * KB)]
        rt = sb("rt", [P, 3, HEADS, HALF], F32, 70.5 * KB)
        negm, rmax, rsum, sx, rden = (sb(n, [P, NT, 2, HEADS], F32, 70.5 * KB + 256 * i)
                                      for i, n in enumerate(("negm", "rmax", "rsum", "sx", "rden")))
        sa = sb("sa", [P, 2, 2 * P], F32, 88 * KB)
        pr = sb("pr", [P, 2, T], F32, 90 * KB)
        ptr = sb("ptr", [P, 2, T], F32, 16 * KB)
        on = sb("on", [P, 2, HEADS * VD], F32, 44 * KB)
        ot = sb("ot", [P, 2 * KO, T], F32, 0)
        oth = sb("oth", [P, 2 * KO, T], F32R, 16 * KB)
        otl = sb("otl", [P, 2 * KO, T], F32R, 32 * KB)
        pa = sb("pa", [P, KD, T], F32, 48 * KB)
        pb = sb("pb", [P, KD, T], F32, 64 * KB)
        x5 = sb("x5", [P, NT, D], F32, 80 * KB)
        h5h = sb("h5h", [P, KD, T], F32R, 0)
        h5l = sb("h5l", [P, KD, T], F32R, 16 * KB)
        sg = nc.alloc_sbuf_tensor_at("sg", [P, 2, T], F32, offset=gain_at)
        mh = sb("mh", [P, KD, T], F32R, 32 * KB)
        ml = sb("ml", [P, KD, T], F32R, 80 * KB)
        x6 = sb("x6", [P, NT, D], F32, 0)
        sq6 = sb("sq6", [P, NT, D], F32, 48 * KB)
        h6 = sb("h6", [P, NT, D], F32, 16 * KB)
        h6t = sb("h6t", [P, KD, T], F32, 64 * KB)
        sel = sb("sel", [P, NT, NB, P], F32R, 32 * KB)
        row_r = sb("row_r", [P, NT, 2, SC], F32R, 83 * KB + 256)
        r_at = [84 * KB]

        def small(name, shape):
            t = sb(name, shape, F32, r_at[0])
            r_at[0] += -(-int(np.prod(shape[1:])) * 4 // 32) * 32
            return t

        lg = small("lg", [P, NT, NR])
        gmax = small("gmax", [P, NT])
        geq = small("geq", [P, NT, NG])
        gcand = small("gcand", [P, NT, NG])
        gmin = small("gmin", [P, NT])
        ghot_r = sb("ghot_r", [P, NT, NG], F32R, 83 * KB)
        ghot = small("ghot", [P, NT, NG])
        gdiff = small("gdiff", [P, NT, NG])
        gexp = small("gexp", [P, NT, NG])
        gsum = small("gsum", [P, NT])
        pgrp = small("pgrp", [P, NT])
        emul = small("emul", [P, NT, NE, NG])
        e8 = small("e8", [P, NT, NE])
        top = [[small(f"{n}{i}", s) for n, s in (("tmax", [P, NT]), ("teq", [P, NT, NE]), ("tcand", [P, NT, NE]),
                                                 ("tmin", [P, NT]), ("thot", [P, NT, NE]))] for i in range(2)]
        e8b = small("e8b", [P, NT, NE])
        wd = [small(f"wd{i}", [P, NT]) for i in range(6)]
        cw = [small(f"cw{i}", [P, NT, NE]) for i in range(2)]
        rowtab = small("rowtab", [P, NT, SC])
        counts = small("counts", [P, NG])
        ovf_n = [small(f"ovf_n{i}", [P, NG]) for i in range(5)]
        incl_m = small("incl_m", [P, NG, NG])
        incl = small("incl", [P, NG])
        soff = small("soff", [P, 2, NG])
        pick = [small(f"pick{i}", [P, NT, NG]) for i in range(3)]
        ranks = [small(f"ranks{i}", [P, NT]) for i in range(7)]
        slot = small("slot", [P, NT])
        ocmp = small("ocmp", [P, NOVF, NG])
        ovf_f = small("ovf_f", [P, NOVF + 1])
        idx_f = small("idx_f", [P, NB])
        whm, wlm = (sb(n, [P, NSPM - NSPL, UNIT], F32R, at) for n, at in (("whm", 28 * KB), ("wlm", 52 * KB)))
        xg = sb("xg", [P, D], F32, 0)
        xgh = sb("xgh", [P, KD, P], F32R, 4 * KB)
        xgl = sb("xgl", [P, KD, P], F32R, 8 * KB)
        yb = sb("yb", [P, D], F32, 12 * KB)
        sgm = sb("sgm", [P, 2, FE], F32, 16 * KB)
        hp = sb("hp", [P, 2, FE], F32, 18 * KB)
        hw = sb("hw", [P, 2, FE], F32, 20 * KB)
        hth = sb("hth", [P, 2, 2, P], F32R, 22 * KB)
        htl = sb("htl", [P, 2, 2, P], F32R, 24 * KB)
        wslot = sb("wslot", [P, SC], F32, 26 * KB)
        ib = sb("ib", [P, 1], I32, 27 * KB)
        ib_g = sb("ib_g", [P, 1], I32, 27 * KB + 64)
        held = sb("held", [1, 1], F32, 27 * KB + 128)
        y8 = sb("y8", [P, NT, D], F32, 28 * KB)

        ps = [ctx.enter_context(nc.psum_tensor(f"ps{i}", [P, 512], F32)) for i in range(8)]

        names = """hi_done lo_done unit_used small_in sq1_done v1_done rstd1_done h1_done h1_ps h1h_done
            h1l_done z1_ps z1_ev z2_ps z2_act z2_dve sqz_done v2_done rstd2_done c_done c_ps ch_done cl_done rope_k
            qkv_ps q_copied v_copied kn_copied q_roped k_ready qk_ps qt_ev kt_ev s_ps bias_done negm_done exp_done
            pt_ps pt_act pt_dve pv_done sx_done sexp_done rden_done on_done ot_ps ot_done oth_done otl_done x5_in h5_done
            h5_ps h5h_done h5l_done pa_ps pa_act pa_dve pb_ps pb_act pb_dve ga_ps ga_sig ga_mul gb_ps gb_sig gb_mul
            mix_done mh_done ml_done x6_in xo_ps xn_done gain2_in xst sq6_done v6_done rstd6_done h6_done h6_st h6_ps
            h6t_done lg_ps ghot_ready gd_ready gexp_done td_ready texp_done rank_ps sel_done slot_ps routed
            gath_in xg_ps xgh_done xgl_done sig_done hw_done ht_ps hth_done htl_done y_ev ib_done ibg_done scat_done held
            wslot_done xg_zero moe_done x8_in y8_in x8_done dve_chain ended""".split()
        S = {n: sem(n) for n in names}
        raw_full = [sem(f"raw_full{i}") for i in range(NRAW)]
        layer_go = sem("layer_go")
        pos_in, x_in, xcopy, x_saved, cst_pool, cst_step, pre_dve, trig_in, trig_done = (sem(n) for n in (
            "pos_in", "x_in", "xcopy", "x_saved", "cst_pool", "cst_step", "pre_dve", "trig_in", "trig_done"))
        fin_sem = {n: sem("fin_" + n) for n in "gain_in sq v rstd h st".split()}

        block = ctx.enter_context(nc.Block())

        def split_place(n, dense, more):
            if n < ND:
                return dense[:, n % NSPL, :]
            i = (n - ND) % NSPM
            return dense[:, (ND + i) % NSPL, :] if i < NSPL else more[:, i - NSPL, :]

        def hi_at(n):
            return split_place(n, wh, whm)

        def lo_at(n):
            return split_place(n, wl, wlm)

        def pieces(n, at, is_raw=False):
            if n >= ND:
                return [at]
            _, _, nk, _, cols = plan[n]
            if n >= U_Z1[1]:
                return [at[:, 0:nk * cols]]
            order = "p (g j d) -> p g j d" if is_raw else "p (j g d) -> p g j d"
            got = []
            for k in range(nk):
                o = k * cols
                got.append(at[:, o:o + AQ].rearrange(order, g=A_KV, d=A_DIM))
                got.append(at[:, o + AQ:o + cols])
            return got

        def product_ready(eng, signal, m, groups, units):
            if m < groups - 1:
                eng.wait_ge(S[signal], m + 1)
            else:
                eng.wait_ge(S["unit_used"], units[1])

        BASE = {"xg_ps": 2, "y_ev": 2, "htl_done": 1, "xgl_done": 1, "hw_done": 3, "held": 1}

        def start_above_zero(eng, *which):
            for n in which:
                eng.sem_inc(S[n], BASE[n])

        def fence(eng, layer, clears=False):
            eng.drain().then_inc(S["ended"], 1)
            if clears:
                eng.wait_ge(S["ended"], 5)
                for s in list(S.values()) + raw_full:
                    eng.sem_clear(s)
                eng.sem_inc(layer_go, 1)
            else:
                eng.wait_ge(layer_go, layer + 1)

        def overflow(eng, body):
            eng.wait_ge(S["routed"], 2)
            novf = eng.value_load(ovf_i[0:1, NOVF:NOVF + 1], min_val=0, max_val=NOVF)
            with eng.Fori(0, NOVF) as j:
                with eng.If(novf > j):
                    body(j + NG, None if eng is not nc.sync else
                         eng.value_load(ovf_i[0:1, bass.ds(j, 1)], min_val=0, max_val=NG - 1))
                    eng.nop()
                with eng.Else():
                    eng.nop()
            return novf + NG

        def blocks(eng, body):
            with eng.Fori(0, NG) as b:
                body(b, b)
            return overflow(eng, body)

        def chained_blocks(eng, body):
            with eng.Fori(0, NG - 1) as b:
                body(b, prepared=True, prepare=True)
            body(NG - 1, prepared=True, prepare=False)
            overflow(eng, lambda b, _: body(b, prepared=False, prepare=False))

        def in_step(split, b, prepared, prepare, at_step):
            done = AHEAD if prepared else 0
            for i in range(NU):
                upto = min(i + AHEAD + 1, NU + AHEAD if prepare else NU)
                for u in range(done, upto):
                    if u < NU:
                        split(ND + u, b)
                    else:
                        split(ND + u - NU, b + 1)
                done = max(done, upto)
                at_step(i)

        sig_at = {unit_at["up", e, 1]: e for e in range(NE)}
        turn_at = {unit_at["down", e - 1, 0] if e else unit_at["up", 1, 0]: e for e in range(NE)}

        @block.sync
        def _(sp):
            sp.dma_start(posc_i[:, :], positions.rearrange("a (t p) -> p (a t)", p=P),
                         allow_slow_non_contiguous=True).then_inc(pos_in, 16)
            sp.dma_start(posr_i[:, :], positions[0].partition_broadcast(P)).then_inc(pos_in, 16)
            sp.dma_start(xl[:, :, :], tiles(x[0])).then_inc(x_in, 16)
            sp.sem_inc(x_saved, 1)

            def room(n, b=0):
                if isinstance(b, int):
                    if n >= NRAW:
                        sp.wait_ge(S["lo_done"], n - NRAW + 1)
                else:
                    sp.wait_ge(S["lo_done"], b * NU + (n - NRAW + 1))

            with sp.Fori(0, L) as l:
                sp.dma_start(gain[:, :], norm_mix[l].partition_broadcast(P)).then_inc(S["small_in"], 16)
                sp.dma_start(gc[:, 0:KQ], q_norm[l].rearrange("(k p) -> p k", p=P),
                             allow_slow_non_contiguous=True).then_inc(S["small_in"], 16)
                sp.dma_start(gc[:, KQ:KC], kv_norm[l].rearrange("(k p) -> p k", p=P),
                             allow_slow_non_contiguous=True).then_inc(S["small_in"], 16)
                sp.dma_start(sink[:, :], sinks[l].partition_broadcast(P)).then_inc(S["small_in"], 16)
                sp.dma_start(bg[:, :], b_gate[l].rearrange("(k p) -> p k", p=P),
                             allow_slow_non_contiguous=True).then_inc(S["small_in"], 16)
                sp.dma_start(br[:, 0:NG], b_group[l].partition_broadcast(P)).then_inc(S["small_in"], 16)
                sp.dma_start(br[:, NG:NR], b_er[l].partition_broadcast(P)).then_inc(S["small_in"], 16)
                sp.dma_start(wr[:, :, 0:NG], w_group[l].rearrange("(k p) n -> p k n", p=P)).then_inc(S["small_in"], 16)
                sp.dma_start(wr[:, :, NG:NR], w_er[l].rearrange("(k p) n -> p k n", p=P)).then_inc(S["small_in"], 16)
                for n, (w, k0, nk, c0, cols) in enumerate(plan):
                    room(n)
                    sp.dma_start(raw[:, n % NRAW, 0:nk * cols].rearrange("p (k n) -> p k n", k=nk),
                                 w[l, k0 * P:(k0 + nk) * P, c0:c0 + cols].rearrange("(k p) n -> p k n", p=P)
                                 ).then_inc(raw_full[n % NRAW], 32)

                def load_block(b, g):
                    for i, (kind, e, half) in enumerate(moe_units):
                        n = ND + i
                        room(n, b)
                        dst, got = raw[:, n % NRAW, :], raw_full[n % NRAW]
                        ex = g * NE + e
                        if kind == "up":
                            kh = KD // 2
                            for j, w in enumerate((w1, w3)):
                                src = w[l].rearrange("e (p k) f -> e p k f", k=KD)
                                sp.dma_start(dst.rearrange("p (j k f) -> p j k f", j=2, k=kh)[:, j],
                                             src[bass.ds(ex, 1), :, half * kh:(half + 1) * kh, :]
                                             .rearrange("o p k f -> (o p) k f")).then_inc(got, 16)
                        else:
                            src = w2[l].rearrange("e (k p) n -> e p k n", p=P)
                            sp.dma_start(dst.rearrange("p (k n) -> p k n", k=FE // P),
                                         src[bass.ds(ex, 1)].rearrange("o p k n -> (o p) k n")).then_inc(got, 32)

                blocks(sp, load_block)
                sp.wait_ge(S["x8_done"], NT)
                sp.dma_start(tiles(xres), xl[:, :, :]).then_inc(x_saved, 16)
                fence(sp, l, clears=True)
            sp.wait_ge(x_saved, L * 16 + 1)

        @block.gpsimd
        def _(pool):
            nc.gpsimd.memset(ident[:, :], 0.0).then_inc(cst_step, 1)
            nc.gpsimd.memset(ones[:, :], 1.0).then_inc(cst_step, 1)
            nc.gpsimd.memset(lower8[:, :, :], 1.0).then_inc(cst_step, 1)
            nc.gpsimd.memset(rowsel[:, :], 0.0).then_inc(cst_step, 1)
            pool.wait_ge(cst_step, 4)
            nc.gpsimd.affine_select(out=ident[:, :], in_=ident[:, :], compare_op=ALU.not_equal, fill=1.0, base=0,
                                    pattern=[[-1, P]], channel_multiplier=1)
            nc.gpsimd.affine_select(out=upper[:, :], in_=ones[:, :], compare_op=ALU.is_gt, fill=0.0, base=0,
                                    pattern=[[1, P]], channel_multiplier=-1)
            nc.gpsimd.affine_select(out=lower8[:, :, :], in_=lower8[:, :, :], compare_op=ALU.is_ge, fill=0.0, base=0,
                                    pattern=[[1, NG], [-1, NG]], channel_multiplier=0)
            nc.gpsimd.memset(rowsel[:, 0:CHUNK], 1.0)
            nc.gpsimd.memset(negrow[:, :], NEG)
            for i in range(HALF):
                f = np.float32(ROPE_THETA) ** (-np.float32(i) / np.float32(HALF))
                nc.gpsimd.memset(invf[:, i:i + 1], float(f))
            nc.gpsimd.iota(iota_p[:, :], [[1, P]], base=0, channel_multiplier=0, allow_small_or_imprecise_dtypes=True)
            nc.gpsimd.iota(iota8[:, :], [[1, NG]], base=0, channel_multiplier=0, allow_small_or_imprecise_dtypes=True)
            nc.gpsimd.iota(iota3[:, :], [[1, NOVF]], base=0, channel_multiplier=0,
                           allow_small_or_imprecise_dtypes=True)
            nc.gpsimd.memset(idx[:, NB:NB + 1], 4096)
            nc.gpsimd.iota(tokid[:, :], [[P, NT]], base=0, channel_multiplier=1,
                           allow_small_or_imprecise_dtypes=True).then_inc(cst_pool, 1)
            pool.wait_ge(cst_pool, 1)
            pool.wait_ge(x_in, 16)
            pool.dma_start(tiles(xres), xl[:, :, :]).then_inc(xcopy, 16)
            pool.wait_ge(xcopy, 16)
            last_row = pool.to_reg(T - 1)
            with pool.Fori(0, L) as l:
                pool.wait_ge(S["pv_done"], NT * 2 * HEADS)
                pool.wait_ge(S["pt_dve"], NT * HEADS)
                pool.wait_ge(S["pt_act"], NT * HEADS)
                pool.dma_start(x5[:, :, :], tiles(xres)).then_inc(S["x5_in"], 16)
                pool.wait_ge(S["unit_used"], U_GB[1])
                pool.dma_start(x6[:, :, :], tiles(xres)).then_inc(S["x6_in"], 16)
                pool.wait_ge(S["mh_done"], KD)
                pool.wait_ge(S["gb_mul"], KD)
                pool.dma_start(gain[:, :], norm_ffn[l].partition_broadcast(P)).then_inc(S["gain2_in"], 16)
                pool.wait_ge(S["xn_done"], 2 * NT)
                pool.dma_start(tiles(xres), x6[:, :, :]).then_inc(S["xst"], 16)
                pool.wait_ge(S["h6_done"], NT)
                pool.dma_start(tiles(hrows), h6[:, :, :]).then_inc(S["h6_st"], 16)
                pool.wait_ge(S["h6_st"], 16)
                pool.wait_ge(S["xst"], 16)
                pool.wait_ge(S["routed"], 2)
                pool.wait_ge(S["h6t_done"], KD)
                pool.wait_ge(S["sq6_done"], NT)

                def hold(b, k):
                    pool.wait_ge(S["held"], b * 3 + (k + BASE["held"]))
                    nc.gpsimd.tensor_tensor(held[:, :], ident[0:1, 0:1], ident[0:1, 1:2], ALU.add).then_inc(S["held"], 1)

                def gather():
                    pool.indirect_dma_start(out=xg[:, :], out_offset=None, in_=hrows,
                                            in_offset=bass.IndirectOffsetOnAxis(ap=ib_g[:, 0:1], axis=0),
                                            bounds_check=last_row, oob_is_err=False).then_inc(S["gath_in"], 16)

                def move_block(b, _):
                    pool.wait_ge(S["gath_in"], b * 16 + 16)
                    hold(b, 0)
                    nc.gpsimd.tensor_copy(ib[:, :], idx[:, bass.ds(b, 1)]).then_inc(S["ib_done"], 1)
                    nc.gpsimd.tensor_copy(ib_g[:, :], idx[:, bass.ds(b + 1, 1)]).then_inc(S["ibg_done"], 1)
                    pool.wait_ge(S["ib_done"], b + 1)
                    pool.wait_ge(S["ibg_done"], b + 2)
                    pool.wait_ge(S["xg_ps"], b * 2 + (2 + BASE["xg_ps"]))
                    hold(b, 1)
                    gather()
                    pool.wait_ge(S["y_ev"], b * 2 + (2 + BASE["y_ev"]))
                    hold(b, 2)
                    pool.indirect_dma_start(out=yrows, out_offset=bass.IndirectOffsetOnAxis(ap=ib[:, 0:1], axis=0),
                                            in_=yb[:, :], in_offset=None,
                                            bounds_check=last_row, oob_is_err=False).then_inc(S["scat_done"], 16)
                    pool.wait_ge(S["scat_done"], b * 16 + 16)

                nc.gpsimd.memset(xg[:, :], 0.0).then_inc(S["xg_zero"], 1)
                pool.wait_ge(S["xg_zero"], 1)
                pool.wait_ge(S["h6_st"], 16)
                pool.wait_ge(S["routed"], 2)
                nc.gpsimd.tensor_copy(ib_g[:, :], idx[:, 0:1]).then_inc(S["ibg_done"], 1)
                pool.wait_ge(S["ibg_done"], 1)
                gather()
                pool.dma_start(xl[:, :, :], tiles(xres)).then_inc(S["x8_in"], 16)
                start_above_zero(pool, "held")
                n_blocks = blocks(pool, move_block)
                pool.wait_ge(S["gath_in"], n_blocks * 16 + 16)
                hold(n_blocks, 0)
                nc.gpsimd.memset(ib[:, :], 0).then_inc(S["moe_done"], 1)
                pool.wait_ge(S["moe_done"], 1)
                pool.dma_start(y8[:, :, :], tiles(yrows)).then_inc(S["y8_in"], 16)
                for n in ("x5_in", "x6_in", "gain2_in", "x8_in", "y8_in"):
                    pool.wait_ge(S[n], 16)
                pool.dma_reset()
                fence(pool, l)
            pool.dma_start(gain[:, :], norm_final.partition_broadcast(P)).then_inc(fin_sem["gain_in"], 16)
            pool.wait_ge(fin_sem["h"], NT)
            pool.dma_start(tiles(out[0]), x1[:, :, :]).then_inc(fin_sem["st"], 16)
            pool.wait_ge(fin_sem["st"], 16)

        @block.scalar
        def _(act):
            act.wait_ge(trig_in, 2)
            nc.scalar.activation(sin[:, :, :], trig[4][:, :, :], ACT.Sin).then_inc(trig_done, 1)
            nc.scalar.activation(cos[:, :, :], trig[5][:, :, :], ACT.Sin).then_inc(trig_done, 1)
            act.wait_ge(trig_done, 2)

            def hi_unit(n, b=0):
                place = n % NRAW
                act.wait_ge(raw_full[place], 32 * (n // NRAW + 1) + b * (32 * NU // NRAW))
                if isinstance(b, int) and NSPL <= n < ND + NSPL:
                    act.wait_ge(S["unit_used"], n - NSPL + 1)
                elif n >= ND:
                    act.wait_ge(S["unit_used"], b * NU + (n - NSPM + 1))
                for dst, src in zip(pieces(n, hi_at(n)), pieces(n, raw[:, place, :], True)):
                    last = nc.scalar.activation(dst, src, ACT.Copy)
                last.then_inc(S["hi_done"], 1)

            act.wait_ge(x_in, 16)
            with act.Fori(0, L) as l:
                done = [0]

                def split_to(n):
                    for u in range(done[0], n):
                        hi_unit(u)
                    done[0] = max(n, done[0])

                for t in range(NT):
                    nc.scalar.activation(sq1[:, t, :], xl[:, t, :], ACT.Square, accum_out=ss[:, t:t + 1]
                                         ).then_inc(S["sq1_done"], 1)
                act.wait_ge(S["v1_done"], 1)
                nc.scalar.activation(rstd[:, :], rs[:, :], ACT.Sqrt).then_inc(S["rstd1_done"], 1)
                split_to(2)
                for k in range(KD):
                    act.wait_ge(S["h1_ps"], k + 1)
                    nc.scalar.activation(h1h[:, k, :], ps[k][:, :], ACT.Copy).then_inc(S["h1h_done"], 1)
                split_to(U_Z1[1] + 2)
                for j in range(5):
                    product_ready(act, "z1_ps", j, 5, U_Z1)
                    if j < 4:
                        nc.scalar.activation(aq[:, j, :], ps[j][:, :], ACT.Copy, scale=A_SCALE).then_inc(S["z1_ev"], 1)
                    else:
                        nc.scalar.activation(ak[:, :], ps[j][:, :], ACT.Copy).then_inc(S["z1_ev"], 1)
                split_to(U_Z2[1] + 2)
                for t in range(NT):
                    product_ready(act, "z2_ps", 2 * t, 2 * NT, U_Z2)
                    nc.scalar.activation(z[:, t, 0:ZC // 2], ps[2 * t][:, 0:ZC // 2], ACT.Copy
                                         ).then_inc(S["z2_act"], 1)
                act.wait_ge(xcopy, 16)
                act.wait_ge(x_saved, l * 16 + 1)
                for t in range(NT):
                    act.wait_ge(S["z2_act"], t + 1)
                    act.wait_ge(S["z2_dve"], t + 1)
                    nc.scalar.activation(sqz[:, t, 0:QR], z[:, t, ZQ:ZKV], ACT.Square, accum_out=ss2[:, 0, t:t + 1])
                    nc.scalar.activation(sqz[:, t, QR:], z[:, t, ZKV:ZKR], ACT.Square, accum_out=ss2[:, 1, t:t + 1]
                                         ).then_inc(S["sqz_done"], 1)
                act.wait_ge(S["v2_done"], 1)
                nc.scalar.activation(rstd2[:, :, :], rs2[:, :, :], ACT.Sqrt).then_inc(S["rstd2_done"], 1)
                split_to(U_QKV[1])
                act.wait_ge(S["small_in"], 9 * 16)
                for c in range(KC):
                    act.wait_ge(S["c_ps"], c + 1)
                    nc.scalar.activation(ch[:, c, :], ps[c][:, :], ACT.Copy, scale=gc[:, c:c + 1]
                                         ).then_inc(S["ch_done"], 1)
                for i in range(NT + 1):
                    if i < NT:
                        o = 4 * (i % 2)
                        product_ready(act, "qkv_ps", i, NT, U_QKV)
                        if i >= 2:
                            act.wait_ge(S["qk_ps"], i - 1)
                        hh = HEADS // 2
                        for n in range(2):
                            nc.scalar.activation(qc[i % 2][:, n * hh:(n + 1) * hh, :].rearrange("p h d -> p (h d)"),
                                                 ps[o + n][:, 0:hh * QD], ACT.Copy).then_inc(S["q_copied"], 1)
                        nc.scalar.activation(v[:, i, :], ps[o + 3][:, :], ACT.Copy).then_inc(S["v_copied"], 1)
                    if i >= 1:
                        t, o = i - 1, 4 * ((i - 1) % 2)
                        act.wait_ge(S["qk_ps"], t + 1)
                        for n in range(2):
                            nc.scalar.activation(qt[0:QD, 4 * n:4 * n + 4, t * P:(t + 1) * P],
                                                 ps[o + n][0:QD, :].rearrange("p (h q) -> p h q", h=4), ACT.Copy
                                                 ).then_inc(S["qt_ev"], 1)

                def attn_out(t, br_):
                    act.wait_ge(S["ot_ps"], 2 * t + br_ + 1)
                    nc.scalar.activation(ot[:, br_ * KO:(br_ + 1) * KO, t * P:(t + 1) * P],
                                         ps[5][:, :].rearrange("p (k q) -> p k q", k=KO), ACT.Copy
                                         ).then_inc(S["ot_done"], 1)

                def sink_exp(t):
                    act.wait_ge(S["sx_done"], t + 1)
                    nc.scalar.activation(sx[:, t, 1, :], sx[:, t, 0, :], ACT.Exp).then_inc(S["sexp_done"], 1)

                act.wait_ge(S["kt_ev"], 2 * NT)
                act.wait_ge(S["qk_ps"], NT)
                NUN = NT * 2 * HEADS
                for u in range(NUN + 1):
                    if u < NUN:
                        t, h, b_ = u // (2 * HEADS), (u // 2) % HEADS, u % 2
                        if u % (2 * HEADS) == 2 and t >= 1:
                            sink_exp(t - 1)
                        act.wait_ge(S["negm_done"], u + 1)
                        if u >= 2:
                            act.wait_ge(S["pt_ps"], u - 1)
                        n = (t + 1) * P if b_ else min(t + 1, 2) * P
                        src = ps[u % 3][:, 0:n] if b_ else sa[:, h % 2, 0:n]
                        nc.scalar.activation(pr[:, u % 2, 0:n], src, ACT.Exp, bias=negm[:, t, b_, h:h + 1],
                                             scale=B_SCALE if b_ else 1.0, accum_out=rsum[:, t, b_, h:h + 1]
                                             ).then_inc(S["exp_done"], 1)
                        if u % (2 * HEADS) == 6 and t >= 1:
                            attn_out(t - 1, 0)
                            attn_out(t - 1, 1)
                    w = u - 1
                    if w >= 0 and w % 2 == 0:
                        t = w // (2 * HEADS)
                        n = min(t + 1, 2) * P
                        act.wait_ge(S["pt_ps"], w + 1)
                        if w >= 2:
                            act.wait_ge(S["pv_done"], w - 1)
                        nc.scalar.activation(ptr[:, w % 2, 0:n], ps[3 + w % 2][:, 0:n], ACT.Copy
                                             ).then_inc(S["pt_act"], 1)
                sink_exp(NT - 1)
                attn_out(NT - 1, 0)
                attn_out(NT - 1, 1)

                act.wait_ge(S["ot_done"], 2 * NT)
                act.wait_ge(S["pv_done"], NUN)
                for k in range(2 * KO):
                    nc.scalar.activation(oth[:, k, :], ot[:, k, :], ACT.Copy).then_inc(S["oth_done"], 1)
                split_to(U_OA[1] + 2)
                for m in range(0, KD, 2):
                    product_ready(act, "pa_ps", m, KD, U_OA)
                    nc.scalar.activation(pa[:, m, :], ps[m][:, :], ACT.Copy).then_inc(S["pa_act"], 1)
                split_to(U_OB[1] + 2)
                for m in range(0, KD, 2):
                    product_ready(act, "pb_ps", m, KD, U_OB)
                    nc.scalar.activation(pb[:, m, :], ps[m][:, :], ACT.Copy).then_inc(S["pb_act"], 1)
                for k in range(KD):
                    act.wait_ge(S["h5_ps"], k + 1)
                    nc.scalar.activation(h5h[:, k, :], ps[k][:, :], ACT.Copy).then_inc(S["h5h_done"], 1)
                split_to(U_GA[1] + 2)
                for m in range(KD):
                    product_ready(act, "ga_ps", m, KD, U_GA)
                    if m >= 2:
                        act.wait_ge(S["ga_mul"], m - 1)
                    nc.scalar.activation(sg[:, m % 2, :], ps[m][:, :], ACT.Sigmoid, bias=bg[:, m:m + 1]
                                         ).then_inc(S["ga_sig"], 1)
                split_to(U_GB[1] + 2)
                for m in range(KD + 1):
                    if m < KD:
                        product_ready(act, "gb_ps", m, KD, U_GB)
                        if m < 2:
                            act.wait_ge(S["ga_mul"], KD)
                        else:
                            act.wait_ge(S["gb_mul"], m - 1)
                        nc.scalar.activation(sg[:, m % 2, :], ps[m][:, :], ACT.Sigmoid, bias=bg[:, KD + m:KD + m + 1]
                                             ).then_inc(S["gb_sig"], 1)
                    if m >= 1:
                        act.wait_ge(S["mix_done"], m)
                        nc.scalar.activation(mh[:, m - 1, :], pa[:, m - 1, :], ACT.Copy).then_inc(S["mh_done"], 1)
                split_to(U_OUT[1])
                for t in range(NT):
                    act.wait_ge(S["xn_done"], 2 * t + 2)
                    nc.scalar.activation(sq6[:, t, :], x6[:, t, :], ACT.Square, accum_out=ss[:, t:t + 1]
                                         ).then_inc(S["sq6_done"], 1)
                act.wait_ge(S["v6_done"], 1)
                nc.scalar.activation(rstd[:, :], rs[:, :], ACT.Sqrt).then_inc(S["rstd6_done"], 1)
                for k in range(KD):
                    act.wait_ge(S["h6_ps"], k + 1)
                    nc.scalar.activation(h6t[:, k, :], ps[k][:, :], ACT.Copy).then_inc(S["h6t_done"], 1)
                split_to(ND + AHEAD)
                act.wait_ge(S["gd_ready"], 1)
                nc.scalar.activation(gexp[:, :, :], gdiff[:, :, :], ACT.Exp).then_inc(S["gexp_done"], 1)
                act.wait_ge(S["td_ready"], 1)
                nc.scalar.activation(wd[1][:, :], wd[0][:, :], ACT.Exp).then_inc(S["texp_done"], 1)

                def rows_hi(b):
                    for c in range(2):
                        act.wait_ge(S["xg_ps"], b * 2 + (c + 1 + BASE["xg_ps"]))
                        nc.scalar.activation(xgh[:, 4 * c:4 * c + 4, :].rearrange("p k t -> p (k t)"), ps[3 + c][:, :],
                                             ACT.Copy).then_inc(S["xgh_done"], 1)

                def act_block(b, prepared, prepare):
                    if not prepared:
                        rows_hi(b)

                    def step(i):
                        if i in turn_at:
                            e = turn_at[i]
                            if e == NE - 1 and prepare:
                                rows_hi(b + 1)
                            act.wait_ge(S["ht_ps"], b * NE + (e + 1))
                            nc.scalar.activation(hth[:, e % 2, :, :].rearrange("p k t -> p (k t)"), ps[2][:, 0:2 * P],
                                                 ACT.Copy).then_inc(S["hth_done"], 1)
                        if i in sig_at:
                            e = sig_at[i]
                            act.wait_ge(S["unit_used"], b * NU + (ND + i + 1))
                            nc.scalar.activation(sgm[:, e % 2, :], ps[e % 2][:, 0:FE], ACT.Sigmoid
                                                 ).then_inc(S["sig_done"], 1)

                    in_step(hi_unit, b, prepared, prepare, step)
                    act.wait_ge(S["unit_used"], b * NU + (ND + NU))
                    act.wait_ge(S["ib_done"], b + 1)
                    nc.scalar.activation(yb[:, 0:512], ps[5][:, :], ACT.Copy).then_inc(S["y_ev"], 1)

                act.wait_ge(S["routed"], 2)
                act.wait_ge(S["h6_st"], 16)
                rows_hi(0)
                start_above_zero(act, "y_ev")
                chained_blocks(act, act_block)
                fence(act, l)
            for t in range(NT):
                nc.scalar.activation(sq1[:, t, :], xl[:, t, :], ACT.Square, accum_out=ss[:, t:t + 1]
                                     ).then_inc(fin_sem["sq"], 1)
            act.wait_ge(fin_sem["v"], 1)
            nc.scalar.activation(rstd[:, :], rs[:, :], ACT.Sqrt).then_inc(fin_sem["rstd"], 1)

        @block.vector
        def _(dve):
            V = nc.vector
            pre = [0]

            def seq0(ins):
                pre[0] += 1
                ins.then_inc(pre_dve, 1)
                dve.wait_ge(pre_dve, pre[0])

            dve.wait_ge(pos_in, 32)
            dve.wait_ge(cst_pool, 1)
            seq0(V.tensor_copy(posc[:, :], posc_i[:, :]))
            dve.wait_ge(cst_pool, 1)
            seq0(V.tensor_copy(upper_r[:, :], upper[:, :]))
            seq0(V.tensor_copy(ones_r[:, :], ones[:, :]))
            seq0(V.tensor_copy(posr[:, :], posr_i[:, :]))
            for t in range(NT):
                lo = max(t - 1, 0) * P
                n = (t + 1) * P - lo
                seq0(V.tensor_scalar(dist[:, t, 0:n], posr[:, lo:lo + n], posc[:, t:t + 1], None, ALU.subtract))
                seq0(V.scalar_tensor_tensor(dist[:, t, 0:n], dist[:, t, 0:n], -1.0, dist[:, t, 0:n], ALU.mult, ALU.max))
                seq0(V.memset(dist[0:CHUNK, t, n - CHUNK:n], BIG))
                if t:
                    seq0(V.memset(dist[:, t, 0:CHUNK], BIG))
                    seq0(V.memset(dist[CHUNK:P, t, CHUNK:P], BIG))
            for t in range(NT):
                seq0(V.tensor_scalar(ang[:, t, :], invf[:, :], posc[:, t:t + 1], None, ALU.mult))
            turns, r = trig[0], trig[1]
            two_pi = 2 * np.pi
            c1 = 6.28125
            c2 = float(np.float32(np.floor((two_pi - c1) * 2 ** 21) / 2 ** 21))
            c3 = float(np.float32(two_pi - c1 - c2))
            magic = float(1.5 * 2 ** 23)
            seq0(V.tensor_scalar(turns[:, :, :], ang[:, :, :], float(1 / two_pi), magic, ALU.mult, ALU.add))
            seq0(V.tensor_scalar(turns[:, :, :], turns[:, :, :], magic, None, ALU.subtract))
            seq0(V.scalar_tensor_tensor(r[:, :, :], turns[:, :, :], -c1, ang[:, :, :], ALU.mult, ALU.add))
            seq0(V.scalar_tensor_tensor(r[:, :, :], turns[:, :, :], -c2, r[:, :, :], ALU.mult, ALU.add))
            seq0(V.scalar_tensor_tensor(r[:, :, :], turns[:, :, :], -c3, r[:, :, :], ALU.mult, ALU.add))
            lim = float(np.nextafter(np.float32(np.pi), np.float32(0)))
            V.tensor_scalar(trig[4][:, :, :], r[:, :, :], lim, -lim, ALU.min, ALU.max).then_inc(trig_in, 1)
            seq0(V.tensor_scalar(trig[2][:, :, :], r[:, :, :], float(np.pi / 2), -two_pi, ALU.is_gt, ALU.mult))
            seq0(V.scalar_tensor_tensor(trig[3][:, :, :], r[:, :, :], float(np.pi / 2), trig[2][:, :, :],
                                        ALU.add, ALU.add))
            V.tensor_scalar(trig[5][:, :, :], trig[3][:, :, :], lim, -lim, ALU.min, ALU.max).then_inc(trig_in, 1)
            dve.wait_ge(trig_done, 2)

            def lo_unit(n, b=0):
                dve.wait_ge(S["hi_done"], b * NU + (n + 1))
                for dst, src, hi in zip(pieces(n, lo_at(n)), pieces(n, raw[:, n % NRAW, :], True),
                                        pieces(n, hi_at(n))):
                    last = V.tensor_tensor(dst, src, hi.bitcast(F32), ALU.subtract)
                last.then_inc(S["lo_done"], 1)

            def lo_part(dst, full, hi):
                return V.tensor_tensor(dst, full, hi.bitcast(F32), ALU.subtract)

            dve.wait_ge(x_in, 16)
            with dve.Fori(0, L) as l:
                done, steps = [0], [0]

                def split_to(n):
                    for u in range(done[0], n):
                        lo_unit(u)
                    done[0] = max(n, done[0])

                def seq(ins):
                    steps[0] += 1
                    ins.then_inc(S["dve_chain"], 1)
                    dve.wait_ge(S["dve_chain"], steps[0])

                def inverse_mean(vv, sums, res, n, name):
                    seq(V.tensor_scalar(vv, sums, 1.0 / n, EPS, ALU.mult, ALU.add))
                    return V.reciprocal(res, vv)

                dve.wait_ge(S["sq1_done"], NT)
                inverse_mean(vs[:, :], ss[:, :], rs[:, :], D, "").then_inc(S["v1_done"], 1)
                dve.wait_ge(S["rstd1_done"], 1)
                dve.wait_ge(S["small_in"], 9 * 16)
                for t in range(NT):
                    V.scalar_tensor_tensor(x1[:, t, :], xl[:, t, :], rstd[:, t:t + 1], gain[:, :], ALU.mult, ALU.mult
                                           ).then_inc(S["h1_done"], 1)
                split_to(2)
                for k in range(KD):
                    dve.wait_ge(S["h1h_done"], k + 1)
                    lo_part(h1l[:, k, :], ps[k][:, :], h1h[:, k, :]).then_inc(S["h1l_done"], 1)
                split_to(U_Z2[1])
                for t in range(NT):
                    product_ready(dve, "z2_ps", 2 * t + 1, 2 * NT, U_Z2)
                    V.tensor_copy(z[:, t, ZC // 2:ZC], ps[2 * t + 1][:, 0:ZC - ZC // 2]).then_inc(S["z2_dve"], 1)
                dve.wait_ge(S["sqz_done"], NT)
                seq(V.tensor_scalar(vs2[:, 0, :], ss2[:, 0, :], 1.0 / QR, EPS, ALU.mult, ALU.add))
                seq(V.tensor_scalar(vs2[:, 1, :], ss2[:, 1, :], 1.0 / KVR, EPS, ALU.mult, ALU.add))
                V.reciprocal(rs2[:, :, :], vs2[:, :, :]).then_inc(S["v2_done"], 1)
                k1, k2 = z[:, :, ZKR:ZKR + HALF], z[:, :, ZKR + HALF:ZC]
                tmp = [rt[:, i, 0:NT, :] for i in range(3)]
                dve.wait_ge(S["z2_act"], NT)
                dve.wait_ge(S["z2_dve"], NT)

                def rope(x1_, x2_, c_, s_, tm):
                    seq(V.tensor_tensor(tm[0], x1_, c_, ALU.mult))
                    seq(V.tensor_tensor(tm[1], x2_, s_, ALU.mult))
                    seq(V.tensor_tensor(tm[2], x1_, s_, ALU.mult))
                    seq(V.tensor_tensor(x1_, tm[0], tm[1], ALU.subtract))
                    seq(V.tensor_tensor(tm[0], x2_, c_, ALU.mult))
                    return V.tensor_tensor(x2_, tm[2], tm[0], ALU.add)

                seq(rope(k1, k2, cos[:, :, :], sin[:, :, :], tmp))
                dve.wait_ge(S["rstd2_done"], 1)
                for t in range(NT):
                    V.tensor_scalar(z[:, t, ZQ:ZKV], z[:, t, ZQ:ZKV], rstd2[:, 0, t:t + 1], None, ALU.mult
                                    ).then_inc(S["c_done"], 1)
                    V.tensor_scalar(z[:, t, ZKV:ZKR], z[:, t, ZKV:ZKR], rstd2[:, 1, t:t + 1], None, ALU.mult
                                    ).then_inc(S["c_done"], 1)
                split_to(U_QKV[1])
                for c in range(KC):
                    dve.wait_ge(S["ch_done"], c + 1)
                    V.scalar_tensor_tensor(cl[:, c, :], ps[c][:, :], gc[:, c:c + 1], ch[:, c, :].bitcast(F32),
                                           ALU.mult, ALU.subtract).then_inc(S["cl_done"], 1)
                dve.wait_ge(xcopy, 16)
                dve.wait_ge(x_saved, l * 16 + 1)
                for i in range(NT + 1):
                    if i < NT:
                        o = 4 * (i % 2)
                        product_ready(dve, "qkv_ps", i, NT, U_QKV)
                        if i >= 2:
                            dve.wait_ge(S["qk_ps"], i - 1)
                        V.tensor_copy(kc[i % 2][:, :, 0:NOPE], ps[o + 2][:, :].rearrange("p (h d) -> p h d", h=HEADS)
                                      ).then_inc(S["kn_copied"], 1)
                        V.tensor_copy(kc[i % 2][:, :, NOPE:QD],
                                      z[:, i:i + 1, ZKR:ZC].to_broadcast([P, HEADS, ROPE])).then_inc(S["k_ready"], 1)
                        dve.wait_ge(S["q_copied"], 2 * i + 2)
                        if i:
                            dve.wait_ge(S["q_roped"], i)
                        q = qc[i % 2]
                        rope(q[:, :, NOPE:NOPE + HALF], q[:, :, NOPE + HALF:QD],
                             cos[:, i:i + 1, :].to_broadcast([P, HEADS, HALF]),
                             sin[:, i:i + 1, :].to_broadcast([P, HEADS, HALF]),
                             [rt[:, j, :, :] for j in range(3)]).then_inc(S["q_roped"], 1)
                    if i >= 1:
                        t, o = i - 1, 4 * ((i - 1) % 2)
                        dve.wait_ge(S["qk_ps"], t + 1)
                        for n in range(2):
                            V.tensor_copy(kt[0:QD, 4 * n:4 * n + 4, t * P:(t + 1) * P],
                                          ps[o + 2 + n][0:QD, :].rearrange("p (h q) -> p h q", h=4)
                                          ).then_inc(S["kt_ev"], 1)

                def finish_tile(t):
                    dve.wait_ge(S["negm_done"], 2 * HEADS * (t + 1))
                    V.tensor_tensor(sx[:, t, 0, :], sink[:, :], negm[:, t, 0, :], ALU.add).then_inc(S["sx_done"], 1)
                    dve.wait_ge(S["sexp_done"], t + 1)
                    dve.wait_ge(S["exp_done"], 2 * HEADS * (t + 1))
                    seq(V.tensor_tensor(rsum[:, t, 0, :], rsum[:, t, 0, :], sx[:, t, 1, :], ALU.add))
                    seq(V.reciprocal(rden[:, t, :, :], rsum[:, t, :, :]))
                    dve.wait_ge(S["pv_done"], 2 * HEADS * (t + 1))
                    if t:
                        dve.wait_ge(S["ot_ps"], 2 * t)
                    for i in range(2):
                        V.tensor_tensor(on[:, i, :].rearrange("p (h d) -> p h d", h=HEADS),
                                        ps[6 + i][:, :].rearrange("p (h d) -> p h d", h=HEADS),
                                        rden[:, t, i, :].rearrange("p (h o) -> p h o", o=1)
                                        .to_broadcast([P, HEADS, VD]), ALU.mult).then_inc(S["on_done"], 1)

                dve.wait_ge(S["qk_ps"], NT)
                NUN = NT * 2 * HEADS
                for u in range(NUN + 1):
                    if u < NUN:
                        t, h, b_ = u // (2 * HEADS), (u // 2) % HEADS, u % 2
                        dve.wait_ge(S["s_ps"], u + 1)
                        if b_ == 0:
                            n = min(t + 1, 2) * P
                            if u >= 4:
                                dve.wait_ge(S["exp_done"], u - 3)
                            seq(V.scalar_tensor_tensor(sa[:, h % 2, 0:n], dist[:, t, 0:n], -slopes[h],
                                                       ps[u % 3][:, 0:n], ALU.mult, ALU.add))
                            seq(V.tensor_reduce(rmax[:, t, 0, h:h + 1], sa[:, h % 2, 0:n], AX, ALU.max))
                            V.tensor_scalar(negm[:, t, 0, h:h + 1], rmax[:, t, 0, h:h + 1], sink[:, h:h + 1], -1.0,
                                            ALU.max, ALU.mult).then_inc(S["negm_done"], 1)
                        else:
                            seq(V.tensor_reduce(rmax[:, t, 1, h:h + 1], ps[u % 3][:, 0:(t + 1) * P], AX, ALU.max))
                            V.tensor_scalar(negm[:, t, 1, h:h + 1], rmax[:, t, 1, h:h + 1], -B_SCALE, None,
                                            ALU.mult).then_inc(S["negm_done"], 1)
                    w = u - 1
                    if w >= 0 and w % 2 == 1:
                        t = w // (2 * HEADS)
                        dve.wait_ge(S["pt_ps"], w + 1)
                        if w >= 2:
                            dve.wait_ge(S["pv_done"], w - 1)
                        V.tensor_copy(ptr[:, w % 2, 0:(t + 1) * P], ps[3 + w % 2][:, 0:(t + 1) * P]
                                      ).then_inc(S["pt_dve"], 1)
                    if u % (2 * HEADS) == 1 and u > 1:
                        finish_tile(u // (2 * HEADS) - 1)
                finish_tile(NT - 1)

                for k in range(2 * KO):
                    dve.wait_ge(S["oth_done"], k + 1)
                    lo_part(otl[:, k, :], ot[:, k, :], oth[:, k, :]).then_inc(S["otl_done"], 1)
                split_to(U_OA[1] + 2)
                dve.wait_ge(S["x5_in"], 16)
                for t in range(NT):
                    V.scalar_tensor_tensor(x5[:, t, :], x5[:, t, :], rstd[:, t:t + 1], gain[:, :], ALU.mult, ALU.mult
                                           ).then_inc(S["h5_done"], 1)
                for m in range(1, KD, 2):
                    product_ready(dve, "pa_ps", m, KD, U_OA)
                    V.tensor_copy(pa[:, m, :], ps[m][:, :]).then_inc(S["pa_dve"], 1)
                split_to(U_OB[1] + 2)
                for m in range(1, KD, 2):
                    product_ready(dve, "pb_ps", m, KD, U_OB)
                    V.tensor_copy(pb[:, m, :], ps[m][:, :]).then_inc(S["pb_dve"], 1)
                for k in range(KD):
                    dve.wait_ge(S["h5h_done"], k + 1)
                    lo_part(h5l[:, k, :], ps[k][:, :], h5h[:, k, :]).then_inc(S["h5l_done"], 1)
                dve.wait_ge(S["pa_act"], KD // 2)
                dve.wait_ge(S["pb_act"], KD // 2)
                dve.wait_ge(S["pa_dve"], KD // 2)
                dve.wait_ge(S["pb_dve"], KD // 2)
                split_to(U_GA[1] + 2)
                for m in range(KD):
                    dve.wait_ge(S["ga_sig"], m + 1)
                    V.tensor_tensor(pa[:, m, :], pa[:, m, :], sg[:, m % 2, :], ALU.mult).then_inc(S["ga_mul"], 1)
                split_to(U_GB[1] + 2)
                for m in range(KD + 1):
                    if m < KD:
                        dve.wait_ge(S["gb_sig"], m + 1)
                        V.tensor_tensor(pb[:, m, :], pb[:, m, :], sg[:, m % 2, :], ALU.mult).then_inc(S["gb_mul"], 1)
                        dve.wait_ge(S["gb_mul"], m + 1)
                        dve.wait_ge(S["ga_mul"], m + 1)
                        V.tensor_tensor(pa[:, m, :], pa[:, m, :], pb[:, m, :], ALU.add).then_inc(S["mix_done"], 1)
                    if m >= 1:
                        dve.wait_ge(S["mh_done"], m)
                        lo_part(ml[:, m - 1, :], pa[:, m - 1, :], mh[:, m - 1, :]).then_inc(S["ml_done"], 1)
                split_to(U_OUT[1])
                dve.wait_ge(S["x6_in"], 16)
                for i in range(2 * NT):
                    t, n = i // 2, i % 2
                    product_ready(dve, "xo_ps", i, 2 * NT, U_OUT)
                    V.tensor_tensor(x6[:, t, n * 512:(n + 1) * 512], x6[:, t, n * 512:(n + 1) * 512], ps[i][:, :],
                                    ALU.add).then_inc(S["xn_done"], 1)
                dve.wait_ge(S["sq6_done"], NT)
                inverse_mean(vs[:, :], ss[:, :], rs[:, :], D, "").then_inc(S["v6_done"], 1)
                dve.wait_ge(S["rstd6_done"], 1)
                dve.wait_ge(S["gain2_in"], 16)
                for t in range(NT):
                    V.scalar_tensor_tensor(h6[:, t, :], x6[:, t, :], rstd[:, t:t + 1], gain[:, :], ALU.mult, ALU.mult
                                           ).then_inc(S["h6_done"], 1)

                def bc(ap, n):
                    return ap.rearrange("p (t o) -> p t o", o=1).to_broadcast([P, NT, n])

                def over(ap, n):
                    return ap.rearrange("p (o n) -> p o n", o=1).to_broadcast([P, NT, n])

                def first_max(val, mx, eq, cand, mn, hot):
                    seq(V.tensor_reduce(mx, val, AX, ALU.max))
                    seq(V.tensor_tensor(eq, val, bc(mx, NG), ALU.is_equal))
                    seq(V.scalar_tensor_tensor(cand, eq, -64.0, over(iota8[:, :], NG), ALU.mult, ALU.add))
                    seq(V.tensor_reduce(mn, cand, AX, ALU.min))
                    return V.tensor_tensor(hot, cand, bc(mn, NG), ALU.is_equal)

                split_to(ND + AHEAD)
                dve.wait_ge(S["lg_ps"], 1)
                seq(V.tensor_tensor(lg[:, :, :], ps[0][:, 0:NT * NR].rearrange("p (t n) -> p t n", t=NT),
                                    over(br[:, :], NR), ALU.add))
                gl, el = lg[:, :, 0:NG], lg[:, :, NG:NR].rearrange("p t (g e) -> p t e g", e=NE)
                first_max(gl, gmax[:, :], geq[:, :, :], gcand[:, :, :], gmin[:, :], ghot[:, :, :]
                          ).then_inc(S["ghot_ready"], 1)
                dve.wait_ge(S["ghot_ready"], 1)
                V.tensor_copy(ghot_r[:, :, :], ghot[:, :, :]).then_inc(S["ghot_ready"], 1)
                V.tensor_tensor(gdiff[:, :, :], gl, bc(gmax[:, :], NG), ALU.subtract).then_inc(S["gd_ready"], 1)
                dve.wait_ge(S["ghot_ready"], 1)
                for t in range(NT):
                    seq(V.tensor_tensor(emul[:, t, :, :], el[:, t],
                                        ghot[:, t:t + 1, :].to_broadcast([P, NE, NG]), ALU.mult))
                seq(V.tensor_reduce(e8[:, :, :], emul[:, :, :, :], AX, ALU.add))
                seq(first_max(e8[:, :, :], *(a[:, :] if len(a.shape) == 2 else a[:, :, :] for a in top[0])))
                seq(V.scalar_tensor_tensor(e8b[:, :, :], top[0][4][:, :, :], NEG, e8[:, :, :], ALU.mult, ALU.add))
                seq(first_max(e8b[:, :, :], *(a[:, :] if len(a.shape) == 2 else a[:, :, :] for a in top[1])))
                V.tensor_tensor(wd[0][:, :], top[1][0][:, :], top[0][0][:, :], ALU.subtract).then_inc(S["td_ready"], 1)
                dve.wait_ge(S["rank_ps"], 1)
                prefix = ps[1][:, 0:NT * NG].rearrange("p (t g) -> p t g", t=NT)
                seq(V.tensor_copy(counts[:, :], ps[1][:, NT * NG:(NT + 1) * NG]))
                for i in range(NOVF):
                    seq(V.tensor_scalar(ovf_n[i][:, :], counts[:, :], float(P * (i + 1)), None, ALU.is_gt))
                seq(V.tensor_tensor(ovf_n[3][:, :], ovf_n[0][:, :], ovf_n[1][:, :], ALU.add))
                seq(V.tensor_tensor(ovf_n[4][:, :], ovf_n[3][:, :], ovf_n[2][:, :], ALU.add))
                seq(V.tensor_tensor(incl_m[:, :, :], lower8[:, :, :],
                                    ovf_n[4][:, :].rearrange("p (o g) -> p o g", o=1).to_broadcast([P, NG, NG]),
                                    ALU.mult))
                seq(V.tensor_reduce(incl[:, :], incl_m[:, :, :], AX, ALU.add))
                seq(V.tensor_tensor(soff[:, 1, :], incl[:, :], ovf_n[4][:, :], ALU.subtract))
                seq(V.tensor_scalar(soff[:, 1, :], soff[:, 1, :], float(P), float(P * (NG - 1)), ALU.mult, ALU.add))
                seq(V.tensor_scalar(soff[:, 0, :], iota8[:, :], float(P), None, ALU.mult))
                seq(V.tensor_tensor(pick[0][:, :, :], ghot[:, :, :], prefix, ALU.mult))
                for i in range(2):
                    seq(V.tensor_tensor(pick[1 + i][:, :, :], ghot[:, :, :], over(soff[:, i, :], NG), ALU.mult))
                for i in range(3):
                    seq(V.tensor_reduce(ranks[i][:, :], pick[i][:, :, :], AX, ALU.add))
                seq(V.tensor_scalar(ranks[3][:, :], ranks[0][:, :], float(P), None, ALU.is_ge))
                seq(V.tensor_tensor(ranks[4][:, :], ranks[2][:, :], ranks[1][:, :], ALU.subtract))
                seq(V.tensor_tensor(ranks[5][:, :], ranks[3][:, :], ranks[4][:, :], ALU.mult))
                seq(V.tensor_tensor(ranks[6][:, :], ranks[0][:, :], ranks[1][:, :], ALU.add))
                seq(V.tensor_tensor(slot[:, :], ranks[5][:, :], ranks[6][:, :], ALU.add))
                dve.wait_ge(S["gexp_done"], 1)
                seq(V.tensor_reduce(gsum[:, :], gexp[:, :, :], AX, ALU.add))
                seq(V.reciprocal(pgrp[:, :], gsum[:, :]))
                dve.wait_ge(S["texp_done"], 1)
                seq(V.tensor_scalar(wd[2][:, :], wd[1][:, :], 1.0, None, ALU.add))
                seq(V.reciprocal(wd[3][:, :], wd[2][:, :]))
                seq(V.tensor_tensor(wd[4][:, :], wd[3][:, :], pgrp[:, :], ALU.mult))
                seq(V.tensor_tensor(wd[5][:, :], wd[4][:, :], wd[1][:, :], ALU.mult))
                seq(V.tensor_tensor(cw[0][:, :, :], top[0][4][:, :, :], bc(wd[4][:, :], NE), ALU.mult))
                seq(V.tensor_tensor(cw[1][:, :, :], top[1][4][:, :, :], bc(wd[5][:, :], NE), ALU.mult))
                seq(V.tensor_tensor(rowtab[:, :, 2:SC], cw[0][:, :, :], cw[1][:, :, :], ALU.add))
                seq(V.memset(rowtab[:, :, 1:2], 1.0))
                seq(V.tensor_copy(rowtab[:, :, 0:1], tokid[:, :].rearrange("p (t o) -> p t o", o=1)))
                seq(V.tensor_copy(row_r[:, :, 0, :], rowtab[:, :, :]))
                seq(V.tensor_tensor(row_r[:, :, 1, :], rowtab[:, :, :], row_r[:, :, 0, :].bitcast(F32), ALU.subtract))
                for t in range(NT):
                    for b in range(NB):
                        V.tensor_scalar(sel[:, t, b, :], iota_p[:, :], float(b * P), slot[:, t:t + 1],
                                        ALU.add, ALU.is_equal).then_inc(S["sel_done"], 1)
                seq(V.tensor_tensor(ocmp[:, :, :],
                                    incl[:, :].rearrange("p (o g) -> p o g", o=1).to_broadcast([P, NOVF, NG]),
                                    iota3[:, :].rearrange("p (j o) -> p j o", o=1).to_broadcast([P, NOVF, NG]),
                                    ALU.is_le))
                seq(V.tensor_reduce(ovf_f[:, 0:NOVF], ocmp[:, :, :], AX, ALU.add))
                seq(V.tensor_copy(ovf_f[:, NOVF:NOVF + 1], incl[:, NG - 1:NG]))
                V.tensor_copy(ovf_i[:, :], ovf_f[0:1, :]).then_inc(S["routed"], 1)
                dve.wait_ge(S["slot_ps"], 1)
                both = ps[2][:, 0:NB * 2 * SC].rearrange("p (b h c) -> p h b c", b=NB, h=2)
                seq(V.tensor_copy(slot_tab[:, :, :], both[:, 0]))
                seq(V.tensor_tensor(slot_tab[:, :, :], slot_tab[:, :, :], both[:, 1], ALU.add))
                seq(V.tensor_scalar(idx_f[:, :], slot_tab[:, :, 1], -4096.0, 4096.0, ALU.mult, ALU.add))
                seq(V.tensor_tensor(idx_f[:, :], idx_f[:, :], slot_tab[:, :, 0], ALU.add))
                V.tensor_copy(idx[:, 0:NB], idx_f[:, :]).then_inc(S["routed"], 1)

                def rows_lo(b):
                    for c in range(2):
                        dve.wait_ge(S["xgh_done"], b * 2 + (c + 1))
                        lo_part(xgl[:, 4 * c:4 * c + 4, :].rearrange("p k t -> p (k t)"), ps[3 + c][:, :],
                                xgh[:, 4 * c:4 * c + 4, :].rearrange("p k t -> p (k t)")).then_inc(S["xgl_done"], 1)

                def dve_block(b, prepared, prepare):
                    if not prepared:
                        rows_lo(b)
                    dve.wait_ge(S["hw_done"], b * (2 * NE) + BASE["hw_done"])
                    V.tensor_copy(wslot[:, :], slot_tab[:, bass.ds(b, 1), :].rearrange("p o c -> p (o c)")
                                  ).then_inc(S["wslot_done"], 1)

                    def step(i):
                        if i in turn_at:
                            e = turn_at[i]
                            if e == NE - 1 and prepare:
                                rows_lo(b + 1)
                            dve.wait_ge(S["hth_done"], b * NE + (e + 1))
                            lo_part(htl[:, e % 2, :, :].rearrange("p k t -> p (k t)"), ps[2][:, 0:2 * P],
                                    hth[:, e % 2, :, :].rearrange("p k t -> p (k t)")).then_inc(S["htl_done"], 1)
                        if i in sig_at:
                            e = sig_at[i]
                            if e == 0:
                                dve.wait_ge(S["wslot_done"], b + 1)
                            dve.wait_ge(S["sig_done"], b * NE + (e + 1))
                            V.scalar_tensor_tensor(hp[:, e % 2, :], ps[e % 2][:, 0:FE], wslot[:, 2 + e:3 + e],
                                                   sgm[:, e % 2, :], ALU.mult, ALU.mult).then_inc(S["hw_done"], 1)
                            dve.wait_ge(S["hw_done"], b * (2 * NE) + (2 * e + 1 + BASE["hw_done"]))
                            V.tensor_tensor(hw[:, e % 2, :], hp[:, e % 2, :], ps[e % 2][:, FE:2 * FE], ALU.mult
                                            ).then_inc(S["hw_done"], 1)

                    in_step(lo_unit, b, prepared, prepare, step)
                    dve.wait_ge(S["unit_used"], b * NU + (ND + NU))
                    dve.wait_ge(S["ib_done"], b + 1)
                    V.tensor_copy(yb[:, 512:1024], ps[6][:, :]).then_inc(S["y_ev"], 1)

                start_above_zero(dve, "htl_done", "xgl_done", "hw_done")
                rows_lo(0)
                chained_blocks(dve, dve_block)
                dve.wait_ge(S["x8_in"], 16)
                dve.wait_ge(S["y8_in"], 16)
                for t in range(NT):
                    V.tensor_tensor(xl[:, t, :], xl[:, t, :], y8[:, t, :], ALU.add).then_inc(S["x8_done"], 1)
                fence(dve, l)
            dve.wait_ge(fin_sem["sq"], NT)
            V.tensor_scalar(vs[:, :], ss[:, :], 1.0 / D, EPS, ALU.mult, ALU.add).then_inc(pre_dve, 1)
            dve.wait_ge(pre_dve, pre[0] + 1)
            V.reciprocal(rs[:, :], vs[:, :]).then_inc(fin_sem["v"], 1)
            dve.wait_ge(fin_sem["rstd"], 1)
            dve.wait_ge(fin_sem["gain_in"], 16)
            for t in range(NT):
                V.scalar_tensor_tensor(x1[:, t, :], xl[:, t, :], rstd[:, t:t + 1], gain[:, :], ALU.mult, ALU.mult
                                       ).then_inc(fin_sem["h"], 1)

        @block.tensor
        def _(pe):
            MM = nc.tensor.matmul

            def mm3(dst, lh, ll, rh, rl, first, last):
                MM(dst, lh, rh, start=first, stop=False)
                MM(dst, lh, rl, start=False, stop=False)
                return MM(dst, ll, rh, start=False, stop=last)

            def weights_in(n, b=0):
                pe.wait_ge(S["lo_done"], b * NU + (n + 1))

            pe.wait_ge(cst_pool, 1)
            with pe.Fori(0, L) as l:
                def transpose_rows(src, rows_done, psd, free=None):
                    for k in range(KD):
                        if free:
                            free(k)
                        for t in range(NT):
                            if k == 0:
                                pe.wait_ge(S[rows_done], t + 1)
                            last = nc.tensor.transpose(ps[k][:, t * P:(t + 1) * P], src[:, t, k * P:(k + 1) * P],
                                                       ident[:, :])
                        last.then_inc(S[psd], 1)

                def part(n, k, c0, cols):
                    o = (k - plan[n][1]) * plan[n][4] + c0
                    return hi_at(n)[:, o:o + cols], lo_at(n)[:, o:o + cols]

                def columns_product(units, groups, act_h, act_l, signal, cols_of, free=None):
                    first_k, last_k = plan[units[0]][1], plan[units[1] - 1][1] + plan[units[1] - 1][2] - 1
                    for n in range(*units):
                        weights_in(n)
                        ks = range(plan[n][1], plan[n][1] + plan[n][2])
                        for m in range(groups):
                            if n == units[0] and free:
                                free(m)
                            for k in ks:
                                a, c = cols_of(n, k, m)
                                last = mm3(ps[m][:, :], a, c, act_h(k), act_l(k), k == first_k, k == last_k)
                            if n == units[1] - 1 and m < groups - 1:
                                last.then_inc(S[signal], 1)
                        last.then_inc(S["unit_used"], 1)

                transpose_rows(x1, "h1_done", "h1_ps")
                pe.wait_ge(S["h1l_done"], KD)

                def z1_cols(n, k, m):
                    h_, l_ = part(n, k, 0, NCOL_T)
                    if m == AH // 2:
                        return h_[:, AQ:NCOL_T], l_[:, AQ:NCOL_T]
                    return h_[:, m * P:(m + 1) * P], l_[:, m * P:(m + 1) * P]

                columns_product(U_Z1, 5, lambda k: h1h[:, k, :], lambda k: h1l[:, k, :], "z1_ps", z1_cols)

                def rows_product(units, act_h, act_l, cols, signal, free=None):
                    first_k, last_k = plan[units[0]][1], plan[units[1] - 1][1] + plan[units[1] - 1][2] - 1
                    for n in range(*units):
                        weights_in(n)
                        for i in range(2 * NT):
                            t, half = i // 2, i % 2
                            if n == units[0] and free:
                                free(i)
                            for k in range(plan[n][1], plan[n][1] + plan[n][2]):
                                a, c = part(n, k, half * cols, cols)
                                tok = slice(t * P, (t + 1) * P)
                                last = mm3(ps[i][:, 0:cols], act_h[:, k, tok], act_l[:, k, tok], a, c,
                                           k == first_k, k == last_k)
                            if n == units[1] - 1 and i < 2 * NT - 1:
                                last.then_inc(S[signal], 1)
                        last.then_inc(S["unit_used"], 1)

                rows_product(U_Z2, h1h, h1l, ZC // 2, "z2_ps",
                             free=lambda i: pe.wait_ge(S["z1_ev"], min(i + 1, 5)))
                for c in range(KC):
                    for t in range(NT):
                        if c == 0:
                            pe.wait_ge(S["c_done"], 2 * t + 2)
                            pe.wait_ge(S["z2_act"], NT)
                        last = nc.tensor.transpose(ps[c][:, t * P:(t + 1) * P], z[:, t, ZQ + c * P:ZQ + (c + 1) * P],
                                                   ident[:, :])
                    last.then_inc(S["c_ps"], 1)
                pe.wait_ge(S["cl_done"], KC)
                n0 = U_QKV[0]
                weights_in(U_QKV[1] - 1)
                for i in range(NT + 1):
                    if i < NT:
                        o, tok = 4 * (i % 2), slice(i * P, (i + 1) * P)
                        if i >= 2:
                            pe.wait_ge(S["qt_ev"], 2 * (i - 1))
                            pe.wait_ge(S["kt_ev"], 2 * (i - 1))
                        hq = HEADS // 2 * QD
                        for half in range(2):
                            for k in range(KQ):
                                n = n0 if k < 2 else n0 + 1
                                last = mm3(ps[o + half][:, 0:hq], ch[:, k, tok], cl[:, k, tok],
                                           *part(n, k, half * hq, hq), k == 0, k == KQ - 1)
                        if i == NT - 1:
                            last.then_inc(S["unit_used"], 2)
                        for two in range(2):
                            for k in range(KKV):
                                wk = [w.rearrange("p (h two d) -> p two h d", two=2, d=NOPE)[:, two]
                                      for w in part(n0 + 2, k, 0, HEADS * 2 * NOPE)]
                                last = mm3(ps[o + 2 + two][:, :], ch[:, KQ + k, tok], cl[:, KQ + k, tok], *wk,
                                           k == 0, k == KKV - 1)
                        last.then_inc(S["qkv_ps" if i < NT - 1 else "unit_used"], 1)
                    if i >= 1:
                        t, o = i - 1, 4 * ((i - 1) % 2)
                        pe.wait_ge(S["q_roped"], t + 1)
                        pe.wait_ge(S["k_ready"], t + 1)
                        pe.wait_ge(S["kn_copied"], t + 1)
                        pe.wait_ge(S["v_copied"], t + 1)
                        for h in range(HEADS):
                            nc.tensor.transpose(ps[o + h // 4][0:QD, (h % 4) * P:(h % 4 + 1) * P], qc[t % 2][:, h, :],
                                                ident[:, :])
                        for h in range(HEADS):
                            last = nc.tensor.transpose(ps[o + 2 + h // 4][0:QD, (h % 4) * P:(h % 4 + 1) * P],
                                                       kc[t % 2][:, h, :], ident[:, :])
                        last.then_inc(S["qk_ps"], 1)

                NUN = NT * 2 * HEADS
                pe.wait_ge(S["qt_ev"], 2 * NT)
                pe.wait_ge(S["kt_ev"], 2 * NT)

                def scores(u):
                    t, h, b_ = u // (2 * HEADS), (u // 2) % HEADS, u % 2
                    if u >= 3:
                        pe.wait_ge(S["exp_done"], u - 2)
                    dst, tok = ps[u % 3], slice(t * P, (t + 1) * P)
                    if b_ == 0:
                        k0 = max(t - 1, 0) * P
                        g = h // (AH // A_KV)
                        rows = slice(g * A_DIM, (g + 1) * A_DIM)
                        last = MM(dst[:, 0:(t + 1) * P - k0], aq[rows, h % (AH // A_KV), tok],
                                  ak[rows, k0:(t + 1) * P], start=True, stop=True)
                    else:
                        n = (t + 1) * P
                        MM(dst[:, 0:n], qt[0:QD, h, tok], kt[0:QD, h, 0:n], start=True, stop=True)
                        last = MM(dst[:, n - CHUNK:n], rowsel[:, :], negrow[:, :], start=False, stop=True,
                                  skip_group_check=True)
                    last.then_inc(S["s_ps"], 1)

                def out_tile(t):
                    for i in range(2):
                        pe.wait_ge(S["on_done"], 2 * t + i + 1)
                        if 2 * t + i >= 1:
                            pe.wait_ge(S["ot_done"], 2 * t + i)
                        for k in range(KO):
                            last = nc.tensor.transpose(ps[5][:, k * P:(k + 1) * P], on[:, i, k * P:(k + 1) * P],
                                                       ident[:, :])
                        last.then_inc(S["ot_ps"], 1)

                scores(0)
                scores(1)
                for u in range(NUN + 1):
                    if u + 2 < NUN:
                        scores(u + 2)
                    if u < NUN:
                        t, b_ = u // (2 * HEADS), u % 2
                        nk = t + 1 if b_ else min(t + 1, 2)
                        pe.wait_ge(S["exp_done"], u + 1)
                        if u >= 2:
                            pe.wait_ge(S["pt_dve" if b_ else "pt_act"], u // 2)
                        for k in range(nk):
                            last = nc.tensor.transpose(ps[3 + u % 2][:, k * P:(k + 1) * P],
                                                       pr[:, u % 2, k * P:(k + 1) * P], ident[:, :])
                        last.then_inc(S["pt_ps"], 1)
                    w = u - 1
                    if w >= 0:
                        t, h, b_ = w // (2 * HEADS), (w // 2) % HEADS, w % 2
                        nk = t + 1 if b_ else min(t + 1, 2)
                        pe.wait_ge(S["pt_dve" if b_ else "pt_act"], w // 2 + 1)
                        if t and h == 0:
                            pe.wait_ge(S["on_done"], 2 * t)
                        g = h // (AH // A_KV)
                        for k in range(nk):
                            val = (v[:, k, h * VD:(h + 1) * VD] if b_ else
                                   z[:, t + 1 - nk + k, g * A_DIM:(g + 1) * A_DIM])
                            last = MM(ps[6 + b_][:, h * VD:(h + 1) * VD], ptr[:, w % 2, k * P:(k + 1) * P], val,
                                      start=(k == 0), stop=(k == nk - 1))
                        last.then_inc(S["pv_done"], 1)
                    if u % (2 * HEADS) == 4 and u > 4:
                        out_tile(u // (2 * HEADS) - 1)
                out_tile(NT - 1)

                pe.wait_ge(S["otl_done"], 2 * KO)
                pe.wait_ge(S["on_done"], 2 * NT)

                def plain(n, k, m):
                    return part(n, k, m * P, P)

                columns_product(U_OA, KD, lambda k: oth[:, k, :], lambda k: otl[:, k, :], "pa_ps", plain)

                def moved(a, d):
                    return lambda m: pe.wait_ge(S[d if m % 2 else a], m // 2 + 1)

                columns_product(U_OB, KD, lambda k: oth[:, KO + k, :], lambda k: otl[:, KO + k, :], "pb_ps", plain,
                                free=moved("pa_act", "pa_dve"))
                transpose_rows(x5, "h5_done", "h5_ps", free=moved("pb_act", "pb_dve"))
                pe.wait_ge(S["h5l_done"], KD)
                columns_product(U_GA, KD, lambda k: h5h[:, k, :], lambda k: h5l[:, k, :], "ga_ps", plain)
                columns_product(U_GB, KD, lambda k: h5h[:, k, :], lambda k: h5l[:, k, :], "gb_ps", plain,
                                free=lambda m: pe.wait_ge(S["ga_sig"], m + 1))
                pe.wait_ge(S["ml_done"], KD)
                rows_product(U_OUT, mh, ml, D // 2, "xo_ps")
                transpose_rows(h6, "h6_done", "h6_ps")
                pe.wait_ge(S["h6t_done"], KD)
                pe.wait_ge(S["small_in"], 9 * 16)
                for t in range(NT):
                    for k in range(KD):
                        last = MM(ps[0][:, t * NR:(t + 1) * NR], h6t[:, k, t * P:(t + 1) * P], wr[:, k, :],
                                  start=(k == 0), stop=(k == KD - 1))
                last.then_inc(S["lg_ps"], 1)
                pe.wait_ge(S["ghot_ready"], 2)
                for t in range(NT + 1):
                    for s_ in range(min(t + 1, NT)):
                        own = s_ == t
                        last = MM(ps[1][:, t * NG:(t + 1) * NG], (upper_r if own else ones_r)[:, :], ghot_r[:, s_, :],
                                  start=(s_ == 0), stop=(s_ == min(t, NT - 1)))
                last.then_inc(S["rank_ps"], 1)
                pe.wait_ge(S["sel_done"], NT * NB)
                for b in range(NB):
                    for t in range(NT):
                        last = MM(ps[2][:, b * 2 * SC:(b + 1) * 2 * SC], sel[:, t, b, :],
                                  row_r[:, t, :, :].rearrange("p h c -> p (h c)"),
                                  start=(t == 0), stop=(t == NT - 1))
                last.then_inc(S["slot_ps"], 1)
                pe.wait_ge(S["routed"], 2)

                def rows_turned(b):
                    pe.wait_ge(S["gath_in"], b * 16 + 16)
                    for c in range(2):
                        pe.wait_ge(S["xgl_done"], b * 2 + (c + BASE["xgl_done"]))
                        for k in range(4):
                            last = nc.tensor.transpose(ps[3 + c][:, k * P:(k + 1) * P],
                                                       xg[:, :].rearrange("t (p k) -> t k p", k=KD)[:, 4 * c + k],
                                                       ident[:, :])
                        last.then_inc(S["xg_ps"], 1)

                def pe_block(b, prepared, prepare):
                    if not prepared:
                        rows_turned(b)
                    pe.wait_ge(S["xgl_done"], b * 2 + (2 + BASE["xgl_done"]))

                    def up(e, half):
                        n = ND + unit_at["up", e, half]
                        weights_in(n, b)
                        if half == 0:
                            pe.wait_ge(S["hw_done"], b * (2 * NE) + (2 * (e - 1) + BASE["hw_done"]))
                        kh = KD // 2
                        for k in range(kh):
                            kk = half * kh + k
                            ww = [w.rearrange("p (j k f) -> p k j f", j=2, k=kh)[:, k]
                                  for w in (hi_at(n), lo_at(n))]
                            last = mm3(ps[e % 2][:, :], xgh[:, kk, :], xgl[:, kk, :], *ww, kk == 0, kk == KD - 1)
                        last.then_inc(S["unit_used"], 1)

                    def turn(e):
                        pe.wait_ge(S["hw_done"], b * (2 * NE) + (2 * e + 2 + BASE["hw_done"]))
                        pe.wait_ge(S["htl_done"], b * NE + (e + BASE["htl_done"]))
                        for j in range(FE // P):
                            last = nc.tensor.transpose(ps[2][:, j * P:(j + 1) * P], hw[:, e % 2, j * P:(j + 1) * P],
                                                       ident[:, :])
                        last.then_inc(S["ht_ps"], 1)

                    def down(e):
                        n = ND + unit_at["down", e, 0]
                        weights_in(n, b)
                        pe.wait_ge(S["htl_done"], b * NE + (e + 1 + BASE["htl_done"]))
                        if e == 0:
                            pe.wait_ge(S["y_ev"], b * 2 + BASE["y_ev"])
                        for k in range(FE // P):
                            for half in range(2):
                                o = k * D + half * 512
                                last = mm3(ps[5 + half][:, :], hth[:, e % 2, k, :], htl[:, e % 2, k, :],
                                           hi_at(n)[:, o:o + 512], lo_at(n)[:, o:o + 512],
                                           e == 0 and k == 0, e == NE - 1 and k == FE // P - 1)
                        last.then_inc(S["unit_used"], 1)

                    for e in range(NE):
                        up(e, 0)
                        if e >= 2:
                            down(e - 2)
                        if e:
                            turn(e - 1)
                        up(e, 1)
                    down(NE - 2)
                    if prepare:
                        rows_turned(b + 1)
                    turn(NE - 1)
                    down(NE - 1)

                start_above_zero(pe, "xg_ps")
                rows_turned(0)
                chained_blocks(pe, pe_block)
                fence(pe, l)


_INS = ["x", "positions", "norm_mix", "w_in", "sinks", "q_norm", "w_qb", "kv_norm", "w_kvb", "w_gate", "b_gate",
        "w_oa", "w_ob", "w_out", "norm_ffn", "w_group", "b_group", "w_er", "b_er", "w1", "w3", "w2", "norm_final"]


def kernel(**inputs):
    import concourse.bacc as _bacc
    from concourse.bass_utils import run_bass_kernel_spmd as _run

    nc = _bacc.Bacc("TRN2", target_bir_lowering=False, num_devices=1)
    arrays, args = {}, []
    for name in _INS:
        a = np.ascontiguousarray(inputs[name])
        arrays[f"in_{name}"] = a
        args.append(nc.dram_tensor(f"in_{name}", a.shape, mybir.dt.from_np(a.dtype), kind="ExternalInput").ap())
    args.append(nc.dram_tensor("out_0", inputs["x"].shape, F32, kind="ExternalOutput").ap())
    hybrid_trunk(nc, *args)
    r = _run(nc, [arrays], core_ids=[0])
    return r.results[0]["out_0"]
```
